# Optimizing a Trainium2 kernel written in Bass

```python
import math
import jax, jax.numpy as jnp
from jax import lax
import numpy as np

D_MODEL = 1024
BATCH = 1
SEQ = 1024
DEPTH = 2
DEC_BATCH = 8
DEC_SEQ = 1
PAST_LEN = 8192
PAGE_SIZE = 128

N_MIXERS = 2
N_S5_LAYERS = (DEPTH + 1) // 2
N_CONV_LAYERS = DEPTH // 2
S5_WIDTH = D_MODEL
S5_GROUP_CH = 16
S5_GROUPS = S5_WIDTH // S5_GROUP_CH
S5_STATE = 64
D_CONV = D_MODEL
CONV_W = 3
D_FF = 2816
ALPHA = (2.0 * DEPTH) ** 0.25
BETA = (8.0 * DEPTH) ** -0.25
LN_EPS = 1e-5

kernel_name = "hybrid_s5_shortconv_convffn_decode_step"

def layer_norm(x, g, b):
    xf = x.astype(jnp.float32)
    mu = jnp.mean(xf, axis=-1, keepdims=True)
    var = jnp.mean(jnp.square(xf - mu), axis=-1, keepdims=True)
    return ((xf - mu) * lax.rsqrt(var + LN_EPS) * g.astype(jnp.float32) + b.astype(jnp.float32)).astype(x.dtype)

def modulate(x, shift, scale):
    return x * (1.0 + scale[:, None, :]) + shift[:, None, :]

def causal_dwconv(v, buf, w):
    seq = v.shape[1]
    cat = jnp.concatenate([buf.astype(v.dtype), v], axis=1)
    out = sum(w[k] * cat[:, k:k + seq] for k in range(CONV_W))
    return out, cat[:, -(CONV_W - 1):]

def _lin_combine(e1, e2):
    a1, b1 = e1
    a2, b2 = e2
    return a2 * a1, a2 * b1 + b2

def s5_mixer(h, h0_re, h0_im, w_in, lam_re, lam_im, log_dt, b_re, b_im, c_re, c_im, d_skip, w_glu):
    n, seq, _ = h.shape
    f32 = jnp.float32
    u = (h @ w_in).astype(f32).reshape(n, seq, S5_GROUPS, S5_GROUP_CH)
    lam = lax.complex(lam_re.astype(f32), lam_im.astype(f32))
    dt = jnp.exp(log_dt.astype(f32))[:, None]
    a_bar = jnp.exp(lam * dt)
    b_bar = ((a_bar - 1.0) / lam)[..., None] * lax.complex(b_re.astype(f32), b_im.astype(f32))
    bu = jnp.einsum('nlgc,gpc->nlgp', u.astype(jnp.complex64), b_bar)
    h0 = lax.complex(h0_re.astype(f32), h0_im.astype(f32))
    bu = bu.at[:, 0].add(a_bar * h0)
    a_seq = jnp.broadcast_to(a_bar, bu.shape)
    _, states = lax.associative_scan(_lin_combine, (a_seq, bu), axis=1)
    y = (jnp.einsum('nlgp,gcp->nlgc', states.real, c_re.astype(f32))
         - jnp.einsum('nlgp,gcp->nlgc', states.imag, c_im.astype(f32)))
    y = (y + d_skip.astype(f32).reshape(S5_GROUPS, S5_GROUP_CH) * u).reshape(n, seq, S5_WIDTH)
    y = jax.nn.gelu(y).astype(h.dtype)
    z = y @ w_glu
    out = z[..., :D_MODEL] * jax.nn.sigmoid(z[..., D_MODEL:])
    last = states[:, -1]
    return out, last.real, last.imag

def short_conv_mixer(h, buf, w_in, conv_w, w_out):
    z = h @ w_in
    gate_b, gate_c, v = z[..., :D_CONV], z[..., D_CONV:2 * D_CONV], z[..., 2 * D_CONV:]
    conv_out, new_buf = causal_dwconv(gate_c * v, buf, conv_w)
    return (gate_b * conv_out) @ w_out, new_buf

def conv_ffn(h, buf, w_up, conv_w, conv_b, w_down):
    up = h @ w_up
    conv_out, new_buf = causal_dwconv(up, buf, conv_w)
    conv_out = conv_out + conv_b
    val, gate = conv_out[..., :D_FF], conv_out[..., D_FF:]
    return (jax.nn.gelu(gate) * val) @ w_down, new_buf

def trunk(x, c, s5_re, s5_im, conv_buf, ffn_buf, p):
    n = c.shape[0]
    mods = (jax.nn.silu(c) @ p['w_ada'] + p['b_ada']).reshape(n, DEPTH, 2, 3, D_MODEL)
    new_re, new_im, new_conv, new_ffn = [], [], [], []
    for i in range(DEPTH):
        shift, scale, gate = mods[:, i, 0, 0], mods[:, i, 0, 1], mods[:, i, 0, 2]
        h = modulate(x, shift, scale)
        if i % N_MIXERS == 0:
            a = i // N_MIXERS
            m, st_re, st_im = s5_mixer(h, s5_re[a], s5_im[a], p['s5_w_in'][a], p['s5_lam_re'][a], p['s5_lam_im'][a],
                                       p['s5_log_dt'][a], p['s5_b_re'][a], p['s5_b_im'][a], p['s5_c_re'][a],
                                       p['s5_c_im'][a], p['s5_d'][a], p['s5_w_glu'][a])
            new_re.append(st_re)
            new_im.append(st_im)
        else:
            b = i // N_MIXERS
            m, nb = short_conv_mixer(h, conv_buf[b], p['sc_w_in'][b], p['sc_conv_w'][b], p['sc_w_out'][b])
            new_conv.append(nb)
        x = layer_norm(ALPHA * x + gate[:, None, :] * m, p['ln_g'][i, 0], p['ln_b'][i, 0])
        shift, scale, gate = mods[:, i, 1, 0], mods[:, i, 1, 1], mods[:, i, 1, 2]
        h = modulate(x, shift, scale)
        f, fb = conv_ffn(h, ffn_buf[i], p['ffn_w_up'][i], p['ffn_conv_w'][i], p['ffn_conv_b'][i], p['ffn_w_down'][i])
        new_ffn.append(fb)
        x = layer_norm(ALPHA * x + gate[:, None, :] * f, p['ln_g'][i, 1], p['ln_b'][i, 1])
    return x, jnp.stack(new_re), jnp.stack(new_im), jnp.stack(new_conv), jnp.stack(new_ffn)

def setup_inputs(seed: int = 0) -> dict:
    key = jax.random.key(seed)
    ks = jax.random.split(key, 32)
    f32 = jnp.float32

    def nrm(k, shape, std):
        return (jax.random.normal(k, shape, f32) * std).astype(f32)

    d = D_MODEL
    lam_im = (jnp.pi * jnp.arange(S5_STATE, dtype=f32))[None, None, :] + nrm(ks[10], (N_S5_LAYERS, S5_GROUPS, S5_STATE), 0.01)
    sc_w_in = nrm(ks[20], (N_CONV_LAYERS, d, 3 * D_CONV), d ** -0.5)
    sc_w_in = sc_w_in * jnp.concatenate([jnp.ones((2 * D_CONV,), f32), jnp.full((D_CONV,), BETA, f32)])
    ffn_w_up = nrm(ks[23], (DEPTH, d, 2 * D_FF), d ** -0.5)
    ffn_w_up = ffn_w_up * jnp.concatenate([jnp.full((D_FF,), BETA, f32), jnp.ones((D_FF,), f32)])
    s5_w_glu = nrm(ks[17], (N_S5_LAYERS, S5_WIDTH, 2 * d), S5_WIDTH ** -0.5)
    s5_w_glu = s5_w_glu * jnp.concatenate([jnp.full((d,), BETA, f32), jnp.ones((d,), f32)])
    return {
        'x_prompt': nrm(ks[0], (BATCH, SEQ, d), 1.0),
        'x_sample': nrm(ks[1], (DEC_BATCH, DEC_SEQ, d), 1.0),
        'c_prompt': nrm(ks[2], (BATCH, d), 1.0),
        'c_sample': nrm(ks[3], (DEC_BATCH, d), 1.0),
        'state_s5_re': nrm(ks[4], (N_S5_LAYERS, DEC_BATCH, S5_GROUPS, S5_STATE), 0.5),
        'state_s5_im': nrm(ks[5], (N_S5_LAYERS, DEC_BATCH, S5_GROUPS, S5_STATE), 0.5),
        'state_conv': nrm(ks[6], (N_CONV_LAYERS, DEC_BATCH, CONV_W - 1, D_CONV), 1.0),
        'state_ffn': nrm(ks[7], (DEPTH, DEC_BATCH, CONV_W - 1, 2 * D_FF), 0.7),
        'w_ada': nrm(ks[8], (d, DEPTH * 2 * 3 * d), d ** -0.5),
        'b_ada': nrm(ks[9], (DEPTH * 2 * 3 * d,), 0.02),
        's5_w_in': nrm(ks[11], (N_S5_LAYERS, d, S5_WIDTH), BETA * d ** -0.5),
        's5_lam_re': -0.5 + nrm(ks[12], (N_S5_LAYERS, S5_GROUPS, S5_STATE), 0.01),
        's5_lam_im': lam_im,
        's5_log_dt': jax.random.uniform(ks[13], (N_S5_LAYERS, S5_GROUPS), f32, math.log(1e-3), math.log(1e-1)),
        's5_b_re': nrm(ks[14], (N_S5_LAYERS, S5_GROUPS, S5_STATE, S5_GROUP_CH), (2.0 * S5_GROUP_CH) ** -0.5),
        's5_b_im': nrm(ks[15], (N_S5_LAYERS, S5_GROUPS, S5_STATE, S5_GROUP_CH), (2.0 * S5_GROUP_CH) ** -0.5),
        's5_c_re': nrm(ks[16], (N_S5_LAYERS, S5_GROUPS, S5_GROUP_CH, S5_STATE), (2.0 * S5_STATE) ** -0.5),
        's5_c_im': nrm(ks[18], (N_S5_LAYERS, S5_GROUPS, S5_GROUP_CH, S5_STATE), (2.0 * S5_STATE) ** -0.5),
        's5_d': nrm(ks[19], (N_S5_LAYERS, S5_WIDTH), 1.0),
        's5_w_glu': s5_w_glu,
        'sc_w_in': sc_w_in,
        'sc_conv_w': nrm(ks[21], (N_CONV_LAYERS, CONV_W, D_CONV), CONV_W ** -0.5),
        'sc_w_out': nrm(ks[22], (N_CONV_LAYERS, D_CONV, d), BETA * D_CONV ** -0.5),
        'ffn_w_up': ffn_w_up,
        'ffn_conv_w': nrm(ks[24], (DEPTH, CONV_W, 2 * D_FF), CONV_W ** -0.5),
        'ffn_conv_b': nrm(ks[25], (DEPTH, 2 * D_FF), 0.02),
        'ffn_w_down': nrm(ks[26], (DEPTH, D_FF, d), BETA * D_FF ** -0.5),
        'ln_g': 1.0 + nrm(ks[27], (DEPTH, 2, d), 0.02),
        'ln_b': nrm(ks[28], (DEPTH, 2, d), 0.02),
    }

def reference(x_prompt, x_sample, c_prompt, c_sample, state_s5_re, state_s5_im, state_conv, state_ffn,
              w_ada, b_ada, s5_w_in, s5_lam_re, s5_lam_im, s5_log_dt, s5_b_re, s5_b_im, s5_c_re, s5_c_im,
              s5_d, s5_w_glu, sc_w_in, sc_conv_w, sc_w_out, ffn_w_up, ffn_conv_w, ffn_conv_b, ffn_w_down,
              ln_g, ln_b):
    p = {'w_ada': w_ada, 'b_ada': b_ada, 's5_w_in': s5_w_in, 's5_lam_re': s5_lam_re, 's5_lam_im': s5_lam_im,
         's5_log_dt': s5_log_dt, 's5_b_re': s5_b_re, 's5_b_im': s5_b_im, 's5_c_re': s5_c_re, 's5_c_im': s5_c_im,
         's5_d': s5_d, 's5_w_glu': s5_w_glu, 'sc_w_in': sc_w_in, 'sc_conv_w': sc_conv_w, 'sc_w_out': sc_w_out,
         'ffn_w_up': ffn_w_up, 'ffn_conv_w': ffn_conv_w, 'ffn_conv_b': ffn_conv_b, 'ffn_w_down': ffn_w_down,
         'ln_g': ln_g, 'ln_b': ln_b}
    nb = x_prompt.shape[0]
    z_s5 = jnp.zeros((N_S5_LAYERS, nb, S5_GROUPS, S5_STATE), jnp.float32)
    z_conv = jnp.zeros((N_CONV_LAYERS, nb, CONV_W - 1, D_CONV), x_prompt.dtype)
    z_ffn = jnp.zeros((DEPTH, nb, CONV_W - 1, 2 * D_FF), x_prompt.dtype)
    y_prompt, s5re_p, s5im_p, conv_p, ffn_p = trunk(x_prompt, c_prompt, z_s5, z_s5, z_conv, z_ffn, p)
    y_sample, s5re_s, s5im_s, conv_s, ffn_s = trunk(x_sample, c_sample, state_s5_re, state_s5_im,
                                                    state_conv, state_ffn, p)
    return (y_prompt, y_sample, s5re_p, s5im_p, s5re_s, s5im_s, conv_p, conv_s, ffn_p, ffn_s)


_drawn_inputs = setup_inputs


def setup_inputs(seed=0):
    import zlib

    import numpy as np

    out = dict(_drawn_inputs(seed))
    spreads = {}
    factors = {'s5_lam_re': 3.62, 'ffn_conv_b': 8.0}
    for name, (base, spread) in spreads.items():
        noise = np.random.default_rng([zlib.crc32(name.encode()), seed]).standard_normal(out[name].shape)
        drawn = base * np.exp(spread * noise) if base else spread * noise
        out[name] = __import__('jax').numpy.asarray(drawn.astype(out[name].dtype))
    for name, factor in factors.items():
        out[name] = (out[name] * factor).astype(out[name].dtype)
    return out
```

```python
import math
from contextlib import ExitStack

import numpy as np
import concourse.bass as bass
from concourse import mybir

F32 = mybir.dt.float32
F32R = mybir.dt.float32r
I32 = mybir.dt.int32
ALU = mybir.AluOpType
ACT = mybir.ActivationFunctionType

D = 1024
KC = 8
KD = 5
SEQ = 1024
NS = 8
NT = SEQ + NS
TH = NT // 3
PT2 = SEQ - 2 * TH
DFF = 2816
FC = DFF // 128
G = 64
GC = 16
P = 64
NP_ = G // 2
L = 8
NCH = SEQ // L
ALPHA = 4.0 ** 0.25
EPS = 1e-5

ADA0 = 16
NADA = 96 - ADA0

U_S5, U_GLU, U_UP, U_SC = 8, 16, 4, 6
NU = U_S5 + U_GLU + 2 * (FC * 2 + FC) + 8 * 3 + 8
UP_GLU = U_S5
UP_F0 = UP_GLU + U_GLU
UP_SC = UP_F0 + 2 * FC
UP_F1 = UP_SC + 24
N_GLU = U_S5
N_F0 = N_GLU + U_GLU
N_SC = N_F0 + 3 * FC
N_F1 = N_SC + 32
D_F0, D_SC = 0, 24 * (FC // 2)
D_F1 = D_SC + 24 * 4
C_F0, C_SC, C_F1 = 0, FC, FC + 8
PK_WT, PK_CA, PK_BD, PK_CD, PK_ROT = 0, 1024, 2176, 2432, 2688
PK = PK_ROT + 1024
KPH = 9


def bc(ap, shape):
    return ap.to_broadcast(shape)


def trunk_kernel(nc, xT, cT, wada, bada, wstream, lam, bT, cS, dT, h0T, ident, stack, eye16, pmask, lnp,
                 cwf, cwc, stf, stc, yT, sfin, ssm, fb, fs1, cb, cs1):
    ctx = ExitStack()
    with ctx:
        def sem(name):
            return ctx.enter_context(nc.semaphore(name))

        def sb(name, shape, dt=F32, stack=ctx):
            return stack.enter_context(nc.sbuf_tensor(name, shape, dt))

        pack_dram = nc.dram_tensor("s5_pack", (KC, 128, PK), F32, kind="Internal").ap()
        k0_dram = nc.dram_tensor("s5_k0", (KC, 128, 128), F32, kind="Internal").ap()

        HH = sb("HH", [128, KC, NT], F32R)
        HL = sb("HL", [128, KC, NT], F32R)
        RAW = sb("RAW", [128, 2, 1024])
        ew = ExitStack()
        AW = sb("AW", [128, 8, 1024], F32, ew)
        ew.close()
        WH = sb("WH", [128, 4, 1024], F32R)
        WL = sb("WL", [128, 4, 1024], F32R)
        ADA = sb("ADA", [128, 2, 1024])
        MOD = sb("MOD", [128, 96, 9])
        BADA = sb("BADA", [128, 96])
        SC = sb("SC", [128, KC, 9])
        SCP = sb("SCP", [128, KC, 32])
        EVA = sb("EVA", [128, 128])
        STK = sb("STK", [128, 9])
        IDN = sb("IDN", [128, 128])
        ONES = sb("ONES", [128, 128])
        ZERO = sb("ZERO", [128, 1])
        EPST = sb("EPST", [128, 1])
        LNP = sb("LNP", [128, 4, 2, KC])
        LC = sb("LC", [128, 4, KC])
        CWC = sb("CWC", [128, KC, 3])
        STC = sb("STC", [128, KC, 2, NS])
        CB = sb("CB", [128, KC, 10])

        early = ExitStack()
        UALL = sb("UALL", [128, KC, NT], F32, early)
        AP_ = sb("AP_", [128, 2, NP_, KPH], F32, early)
        RHO = sb("RHO", [128, NP_], F32, early)
        H0 = sb("H0", [128, 2, NP_, NS], F32, early)
        SSM = H0
        SFIN = sb("SFIN", [128, 2, NP_], F32, early)
        DSK = sb("DSK", [128, KC], F32, early)
        E16 = sb("E16", [128, GC], F32, early)
        PM = sb("PM", [128, 4, NS], F32, early)
        ea = ExitStack()
        PKA = sb("PKA", [128, PK], F32, ea)
        LAM = sb("LAM", [128, 3, NP_], F32, ea)
        BR = sb("BR", [128, 2, NP_, GC], F32, ea)
        CR = sb("CR", [128, 2, NP_, GC], F32, ea)
        BB = sb("BB", [128, 2, NP_, GC], F32, ea)
        AR = sb("AR", [128, 2, NP_, L], F32, ea)
        UP7 = sb("UP7", [128, 2, 7, NP_], F32, ea)
        Q = sb("Q", [128, 24, NP_], F32, ea)
        QI = sb("QI", [128, NP_], I32, ea)
        BD = sb("BD", [128, 2, 4, 2, GC], F32, ea)
        KR = sb("KR", [128, 128], F32, ea)
        TP = sb("TP", [128, 2, 4 * KPH * GC], F32, ea)
        RP = sb("RP", [128, 256], F32, ea)
        XSB = sb("XSB", [128, SEQ], F32, ea)
        XTB = sb("XTB", [128, SEQ], F32, ea)
        XS = sb("XS", [128, KC, NS], F32, ea)
        HS = sb("HS", [128, KC, NS], F32, ea)
        XIN = [UALL[:, 6, 0:SEQ], XSB[:, :]] + [UALL[:, k, 0:SEQ] for k in range(KC - 2)]
        XT = [UALL[:, 7, 0:SEQ], XTB[:, :]]
        FIRST = [UALL[:, 0:2, 0:1024], UALL[:, 2:4, 0:1024], UALL[:, 4:6, 0:1024], ADA[:, :, :],
                 PKA[:, 0:2048].rearrange("p (a n) -> p a n", a=2), AW[:, 4:6], AW[:, 6:8], AW[:, 2:4]]
        EV = [t[0:9, 512 * i:512 * (i + 1)] for t in (BB[:, :, :, :].rearrange("p a b c -> p (a b c)"),
                                                      TP[:, :, :].rearrange("p a b -> p (a b)")) for i in range(2)]
        RT = [Q[:, 8 * i:8 * (i + 1), :].rearrange("p a b -> p (a b)") for i in range(3)] + [RP[:, :]]
        W2 = BR[:, :, :, :].rearrange("p a b c -> p (a b c)").rearrange("p (a b s c) -> p a b s c", a=2, b=4, s=L)
        ea.close()
        eb = ExitStack()
        PKB = sb("PKB", [128, PK], F32, eb)
        UF = sb("UF", [128, L, NCH], F32, eb)
        UTOK = sb("UTOK", [128, 8, L, GC], F32, eb)
        UT = sb("UT", [128, 8, NCH], F32, eb)
        TQ = sb("TQ", [128, 4, 4, NCH], F32, eb)
        GS = sb("GS", [128, 2, 4, NCH + 1], F32, eb)
        TT = sb("TT", [128, 8, 128], F32, eb)
        UM = sb("UM", [128, 4, NS], F32, eb)
        SQ_ = sb("SQ_", [128, 8, 4 * NS], F32, eb)
        YT = UTOK[:, :, :, :].rearrange("p a b c -> p (a b c)").rearrange("p (s n) -> p s n", s=L)
        eb.close()
        early.close()
        X = sb("X", [128, KC, NT])
        eh = ExitStack()
        HBUF = sb("HBUF", [128, 2, KC, TH], F32, eh)
        HB = [HBUF[:, 0], HBUF[:, 1]]
        eh.close()
        GH = sb("GH", [128, 4, NT], F32R)
        GL = sb("GL", [128, 4, NT], F32R)
        ROWS = sb("ROWS", [128, 4, NT + 2])
        CWF = sb("CWF", [128, FC, 2, 4])
        STF = sb("STF", [128, FC * 2, 2, NS])
        FB = sb("FB", [128, FC * 2, 10])
        FSA = sb("FSA", [128, KC, NS])
        SMP = sb("SMP", [128, 2, KC, NS])
        U0, U1 = ROWS[:, 0, :], ROWS[:, 1, :]
        T0, T1 = ROWS[:, 2, 0:NT], ROWS[:, 3, 0:NT]
        rows_flat = ROWS[:, :, :].rearrange("p a b -> p (a b)")
        LSQ = rows_flat[:, 0:KC * TH].rearrange("p (k t) -> p k t", k=KC)
        SQB = [LSQ, HB[1]]
        LT = rows_flat[:, KC * TH:KC * TH + 4 * TH].rearrange("p (k t) -> p k t", k=4)

        BK = [ctx.enter_context(nc.psum_tensor(f"bank{i}", [128, 512], F32)) for i in range(8)]

        s_cst = sem("first_constants_loaded")
        s_cst2 = sem("constants_loaded")
        s_xin = [sem(f"x_chunk_loaded{i}") for i in range(KC)]
        s_xfree = sem("x_chunk_used")
        s_hx = sem("x_modulated")
        s_silu = sem("silu_c_ready")
        s_c = sem("c_loaded")
        s_first = [sem(f"first_ada_pair_loaded{i}") for i in range(8)]
        s_fprod = sem("first_ada_pair_done")
        s_fev = sem("first_ada_bank_taken")
        s_ftr = sem("first_modulations_transposed")
        s_adain = [sem(f"ada_block_loaded{i}") for i in range(2)]
        s_ada = sem("ada_block_done")
        s_apart = sem("ada_partial_sums_taken")
        s_adaev = sem("first_modulations_ready")
        s_raw = [sem(f"raw_unit_loaded{i}") for i in range(2)]
        s_hi = sem("unit_hi_written")
        s_unit = sem("unit_split")
        s_up = sem("up_bank_done")
        s_ev = sem("up_bank_taken")
        s_down = sem("down_bank_done")
        s_dev = sem("down_bank_taken")
        s_h = sem("h_ready")
        s_ones = sem("masks_ready")
        s_pw = sem("power_tables_ready")
        s_w = sem("state_input_ready")
        s_wt = sem("state_input_transposed")
        s_wtev = sem("state_input_packed")
        s_bd = sem("b_diagonal_ready")
        s_k0 = sem("k0_done")
        s_bdt = sem("b_transposed")
        s_bdtev = sem("b_packed")
        s_kr = sem("k0_taken")
        s_rtab = sem("rotation_half_ready")
        s_rot6 = sem("rotation_packed")
        s_pkr = sem("rotation_stored")
        s_pk = sem("pack_stored")
        s_krd = sem("k0_stored")
        s_uf = sem("u_staged")
        s_tok = sem("u_token_major")
        s_tokev = sem("u_token_major_taken")
        s_ut = sem("u_chunked")
        s_utev = sem("u_chunked_taken")
        s_wtl = sem("wt_loaded")
        s_tl = sem("toeplitz_loaded")
        s_rl = sem("rotation_loaded")
        s_cal = sem("ca_loaded")
        s_e = sem("chunk_inputs_done")
        s_rot = sem("chunk_inputs_taken")
        s_um = sem("masked_u_ready")
        s_bu = sem("sample_inputs_done")
        s_g = sem("states_ready")
        s_tu = sem("toeplitz_done")
        s_y = sem("y_done")
        s_yt = sem("y_gelu_taken")
        s_yb = sem("y_back_done")
        s_hhy = sem("y_hi_written")
        s_ysd = sem("sample_y_summed")
        s_ysg = sem("sample_y_gelu")
        s_hl = sem("y_split")
        s_xl = sem("x_reloaded")
        s_late = sem("late_constants_loaded")
        s_row = sem("rows_used")
        s_conv = sem("gate_conv_ready")
        s_gelu = sem("gelu_ready")
        s_prod = sem("product_ready")
        s_ghi = sem("product_hi_written")
        s_g2 = sem("hidden_chunk_ready")
        s_xr = sem("residual_ready")
        s_mean = sem("mean_done")
        s_cent = sem("centered")
        s_sq = sem("squares_ready")
        s_var = sem("variance_done")
        s_sd = sem("deviation_ready")
        s_xn = sem("normalized")
        s_hh = sem("h_half_modulated")
        s_hhi = sem("h_hi_ready")
        s_hlo = sem("h_lo_by_pool_ready")
        s_xup = sem("alpha_x_ready")
        s_y2 = sem("output_chunk_ready")
        s_st = sem("state_loaded")
        s_out = sem("outputs_stored")
        s_fout = sem("ffn_state_stored")

        N_CST, N_CST2 = 4, 12
        block = ctx.enter_context(nc.Block())

        @block.sync
        def _(sp):
            sp.dma_start(SC[:, :, :], cT).then_inc(s_c, 16)
            for i in range(8):
                sp.dma_start(FIRST[i], wada[2 * i:2 * i + 2, :, :].rearrange("a p n -> p a n")).then_inc(s_first[i], 16)
                if i == 3:
                    for dst, src in ((BADA[:, :], bada), (IDN[:, :], ident), (STK[:, :], stack), (LAM[:, :, :], lam)):
                        sp.dma_start(dst, src).then_inc(s_cst, 16)
            for k in range(2):
                sp.dma_start(XIN[k], xT[:, k, 0:SEQ]).then_inc(s_xin[k], 16)
            sp.wait_ge(s_fprod, 3)
            for k in range(2, KC):
                sp.dma_start(XIN[k], xT[:, k, 0:SEQ]).then_inc(s_xin[k], 16)
            for dst, src in ((XS[:, :, :], xT[:, :, SEQ:NT]), (LNP[:, :, :, :], lnp),
                             (BR[:, 0], bT[0]), (BR[:, 1], bT[1]), (CR[:, 0], cS[0]), (CR[:, 1], cS[1]),
                             (H0[:, :, :, :], h0T), (DSK[:, :], dT), (E16[:, :], eye16),
                             (PM[:, :, :], pmask), (CWC[:, :, :], cwc), (STC[:, :, :, :], stc)):
                sp.dma_start(dst, src).then_inc(s_cst2, 16)

            def load_unit(n, slot):
                sp.wait_ge(s_unit, n - 1)
                sp.dma_start(RAW[:, slot, :], wstream[bass.ds(n, 1), :, :].rearrange("a p n -> p (a n)"))\
                    .then_inc(s_raw[slot], 16)

            def load_ada(u, slot):
                sp.wait_ge(s_ada, u - 1)
                sp.dma_start(ADA[:, slot, :], wada[bass.ds(ADA0 + u, 1), :, :].rearrange("a p n -> p (a n)"))\
                    .then_inc(s_adain[slot], 16)

            for n in range(2):
                sp.dma_start(RAW[:, n, :], wstream[n, :, :]).then_inc(s_raw[n], 16)
            sp.wait_ge(s_fprod, 4)
            for u in range(2):
                sp.dma_start(ADA[:, u, :], wada[ADA0 + u, :, :]).then_inc(s_adain[u], 16)

            load_unit(2, 0)
            load_unit(3, 1)
            with sp.Fori(0, KC // 2) as a:
                for q in range(2):
                    j = 2 * a + q
                    load_unit(j + 4, q)
                    load_ada(j + 2, q)
                    sp.wait_ge(s_kr, j + 1)
                    sp.dma_start(k0_dram[bass.ds(j, 1), :, :].rearrange("a p n -> p (a n)"), KR[:, :]).then_inc(s_krd, 16)
                    sp.wait_ge(s_wtev, 2 * (j + 1))
                    sp.wait_ge(s_bdtev, j + 1)
                    sp.wait_ge(s_bd, j + 1)
                    sp.dma_start(pack_dram[bass.ds(j, 1), :, 0:PK_ROT].rearrange("a p n -> p (a n)"), PKA[:, 0:PK_ROT])\
                        .then_inc(s_pk, 16)
                    sp.wait_ge(s_rot6, j + 1)
                    sp.dma_start(pack_dram[bass.ds(j, 1), :, PK_ROT:PK].rearrange("a p n -> p (a n)"), PKA[:, PK_ROT:PK])\
                        .then_inc(s_pkr, 16)
            sp.wait_ge(s_krd, 16 * KC)
            sp.wait_ge(s_pk, 16 * KC)
            sp.wait_ge(s_pkr, 16 * KC)
            sp.wait_ge(s_ones, 3)

            def load_pack(j, at, n, s):
                sp.dma_start(PKB[:, at:at + n],
                             pack_dram[bass.ds(j, 1), :, at:at + n].rearrange("a p n -> p (a n)")).then_inc(s, 16)

            def s5_loads(j, first):
                if not first:
                    sp.wait_ge(s_e, j)
                load_pack(j, PK_WT, 1024, s_wtl)
                if not first:
                    sp.wait_ge(s_bu, j)
                load_pack(j, PK_BD, 256, s_wtl)
                if not first:
                    sp.wait_ge(s_tu, j)
                kd = k0_dram[bass.ds(j, 1), :, :].rearrange("a (g c) n -> c (a g) n", c=GC)
                for s in range(L):
                    sp.dma_start(TT[GC * s:GC * (s + 1), :, GC * s:128], kd[:, :, 0:128 - GC * s]).then_inc(s_tl, 16)
                if not first:
                    sp.wait_ge(s_g, j)
                load_pack(j, PK_ROT, 1024, s_rl)
                if not first:
                    sp.wait_ge(s_y, j)
                load_pack(j, PK_CA, 1152, s_cal)
                load_pack(j, PK_CD, 256, s_cal)

            s5_loads(0, True)
            with sp.Fori(1, KC) as j:
                s5_loads(j, False)
            sp.wait_ge(s_hl, KC)
            sp.dma_start(sfin, SFIN[:, :, :]).then_inc(s_out, 16)
            sp.dma_start(ssm, SSM[:, :, :, :]).then_inc(s_out, 16)
            sp.wait_ge(s_out, 32)
            sp.dma_start(X[:, :, :], xT).then_inc(s_xl, 16)
            sp.dma_start(CWF[:, :, :, :], cwf[0]).then_inc(s_late, 16)
            sp.dma_start(STF[:, :, :, :], stf[0]).then_inc(s_late, 16)
            with sp.Fori(0, 4) as a:
                for b in range(4):
                    load_unit(12 + 4 * a + b, b % 2)
                    load_ada(10 + 4 * a + b, b % 2)
            with sp.Fori(0, 10) as a:
                for b in range(6):
                    load_unit(28 + 6 * a + b, b % 2)
                    if b < 4:
                        load_ada(26 + 4 * a + b, b % 2)
            for b in range(4):
                load_unit(88 + b, b % 2)
                load_ada(66 + b, b % 2)
            load_unit(92, 0)
            load_unit(93, 1)
            with sp.Fori(0, 5) as a:
                for b in range(2):
                    load_unit(94 + 2 * a + b, b)
                    load_ada(70 + 2 * a + b, b)
            with sp.Fori(52, NU // 2) as a:
                for b in range(2):
                    load_unit(2 * a + b, b)
            sp.wait_ge(s_y2, 1)
            sp.dma_start(cb, CB[:, :, :]).then_inc(s_out, 16)
            sp.dma_start(cs1, STC[:, :, 1, :]).then_inc(s_out, 16)
            sp.dma_start(fb[1], FB[:, :, :]).then_inc(s_out, 16)
            sp.dma_start(fs1[1], STF[:, :, 1, :]).then_inc(s_out, 16)
            for t in range(3):
                sp.wait_ge(s_y2, KC * (t + 1))
                sp.dma_start(yT[:, :, TH * t:TH * (t + 1)], X[:, :, TH * t:TH * (t + 1)]).then_inc(s_out, 16)
            sp.wait_ge(s_out, 16 * 9)

        @block.gpsimd
        def _(pool):
            pool.memset(ZERO[:, :], 0.0)
            pool.memset(EPST[:, :], EPS)
            pool.memset(ONES[:, :], 1.0 / D).then_inc(s_ones, 1)
            pool.drain()
            pool.wait_ge(s_adaev, 1)

            def split_unit(n, slot):
                pool.wait_ge(s_raw[slot % 2], 8 * (n - slot % 2) + 16)
                pool.tensor_tensor(WH[:, slot, :], RAW[:, slot % 2, :], bc(ZERO[:, :], [128, 1024]), ALU.add).then_inc(s_hi, 1)
                pool.wait_ge(s_hi, n + 1)
                pool.tensor_tensor(WL[:, slot, :], RAW[:, slot % 2, :], WH[:, slot, :].bitcast(F32), ALU.subtract)\
                    .then_inc(s_unit, 1)

            R = PKA[:, PK_ROT:PK_ROT + 1024].rearrange("p (a b c) -> p a b c", a=2, b=4)
            pool.memset(R[:, 0, :, 0:1], 1.0)
            pool.memset(R[:, 1, :, 0:1], 0.0)
            pool.drain()

            def rotations(j, first):
                if not first:
                    pool.wait_ge(s_pkr, 16 * j)
                for lv in range(6):
                    m = 1 << lv
                    ur, ui = (bc(UP7[:, pl, lv, bass.ds(4 * j, 4)].unsqueeze(2), [128, 4, m]) for pl in range(2))
                    t = [RT[i][:, 0:4 * m].rearrange("p (a b) -> p a b", a=4) for i in range(4)]
                    pool.tensor_tensor(t[0], R[:, 0, :, 0:m], ur, ALU.mult)
                    pool.tensor_tensor(t[1], R[:, 1, :, 0:m], ui, ALU.mult)
                    pool.tensor_tensor(t[2], R[:, 0, :, 0:m], ui, ALU.mult)
                    pool.tensor_tensor(t[3], R[:, 1, :, 0:m], ur, ALU.mult)
                    pool.drain()
                    pool.tensor_tensor(R[:, 0, :, m:2 * m], t[0], t[1], ALU.subtract)
                    last = pool.tensor_tensor(R[:, 1, :, m:2 * m], t[2], t[3], ALU.add)
                    if lv < 5:
                        pool.drain()
                last.then_inc(s_rtab, 1)

            for n in range(4):
                split_unit(n, n)
            pool.wait_ge(s_pw, 1)
            rotations(0, True)
            pool.wait_ge(s_up, 3)
            split_unit(4, 0)
            for j in range(1, KC):
                rotations(j, False)
                pool.wait_ge(s_up, 3 * (j + 1))
                split_unit(4 + j, j % 4)
            pool.wait_ge(s_krd, 16 * KC)
            pool.wait_ge(s_pk, 16 * KC)
            pool.wait_ge(s_pkr, 16 * KC)
            pool.memset(TT[:, :, :], 0.0).then_inc(s_ones, 1)
            pool.memset(GS[:, :, :, 0:1], 0.0).then_inc(s_ones, 1)
            with pool.Fori(0, 3) as a:
                for b in range(4):
                    pool.wait_ge(s_up, 3 * (4 * a + b) + 3 * 9)
                    split_unit(12 + 4 * a + b, b)

            def users():
                out = [(s_up, 3 * (n + 1)) for n in range(N_F0)]
                def phase(up, dn, groups, ups):
                    seq, u, g = [], up, 0
                    def ups_(k):
                        nonlocal u
                        for _ in range(k):
                            u += 1
                            seq.append((s_up, 3 * u))
                    ups_(ups)
                    seq[0] = seq[1]
                    for g in range(1, groups):
                        ups_(ups)
                        seq.extend([(s_down, dn + 24 * g)] * 2)
                    seq.extend([(s_down, dn + 24 * groups)] * 2)
                    return seq
                out += phase(UP_F0, D_F0, FC // 2, 4)
                out += phase(UP_SC, D_SC, 4, 6)
                out += phase(UP_F1, D_F1, FC // 2, 4)
                return out
            used = users()
            assert len(used) == NU

            def straight(lo, hi):
                for n in range(lo, hi):
                    pool.wait_ge(*used[n - 4])
                    split_unit(n, n % 4)

            def looped(lo, count):
                with pool.Fori(0, count) as a:
                    for q in range(12):
                        s, v = used[lo + q - 4]
                        step = 24 if s is s_up else 48
                        assert used[lo + q - 4 + 12 * (count - 1)] == (s, v + step * (count - 1))
                        pool.wait_ge(s, v + step * a)
                        split_unit(lo + q + 12 * a, (lo + q) % 4)

            def residual(li):
                for t in range(3):
                    c = slice(TH * t, TH * (t + 1))
                    pool.wait_ge(s_hhi, 3 * li + t + 1)
                    pool.tensor_tensor(HL[:, KD:KC, c], HB[t % 2][:, KD:KC], HH[:, KD:KC, c].bitcast(F32), ALU.subtract)\
                        .then_inc(s_hlo, 1)
                    if t == 2:
                        pool.wait_ge(s_h, 3 * li + 3)
                    for k in range(KC):
                        xk = X[:, k, TH * t:TH * (t + 1)]
                        m = pool.tensor_scalar(xk, xk, LC[:, 2, k:k + 1], LC[:, 3, k:k + 1], ALU.mult, ALU.add)
                m.then_inc(s_xup, 1)

            straight(N_F0, N_F0 + 4)
            residual(0)
            straight(N_F0 + 4, N_F0 + 12)
            looped(N_F0 + 12, 4)
            straight(N_F0 + 60, N_SC + 4)
            residual(1)
            straight(N_SC + 4, N_F1 + 4)
            residual(2)
            straight(N_F1 + 4, N_F1 + 12)
            looped(N_F1 + 12, 4)
            straight(N_F1 + 60, NU)

        @block.tensor
        def _(pe):
            def ada_partial(bank, slot, count):
                pe.wait_ge(s_adain[slot], 16 * count)
                for i in (0, 2, 4, 6, 1, 3, 5, 7):
                    g = i // 2
                    m = pe.matmul(bank[32 * g:32 * (g + 1), TH:TH + 128], SCP[:, i, :], ADA[:, slot, 128 * i:128 * (i + 1)],
                                  start=i % 2 == 0, stop=i % 2 == 1, skip_group_check=True)
                m.then_inc(s_ada, 1)

            def ada_sum(bank):
                return pe.matmul(bank[:, TH:TH + 9], EVA[:, :], STK[:, :], start=True, stop=True, skip_group_check=True)

            def up_unit(n, slot, u, wait_bank=True, ada=None):
                pe.wait_ge(s_unit, n + 1)
                par = slot % 2
                if ada is not None:
                    if wait_bank:
                        pe.wait_ge(s_ev, 3 * u - 3)
                    ada_partial(BK[3 * par + 2], par, ada)
                for t in range(3):
                    if wait_bank:
                        pe.wait_ge(s_ev, 3 * u + t - 5)
                    if t == 2 and ada is not None:
                        pe.wait_ge(s_apart, u + 1)
                    o = BK[3 * par + t][:, 0:TH]
                    for k in range(KC):
                        wh = WH[:, slot, 128 * k:128 * (k + 1)]
                        wl = WL[:, slot, 128 * k:128 * (k + 1)]
                        hh, hl = HH[:, k, TH * t:TH * (t + 1)], HL[:, k, TH * t:TH * (t + 1)]
                        pe.matmul(o, wh, hh, start=k == 0, stop=False)
                        pe.matmul(o, wh, hl, start=False, stop=False)
                        m = pe.matmul(o, wl, hh, start=False, stop=k == KC - 1)
                    if t == 2 and ada is not None:
                        m = ada_sum(BK[3 * par + 2])
                    m.then_inc(s_up, 1)

            pe.wait_ge(s_silu, 1)
            for i in range(8):
                pe.wait_ge(s_first[i], 16)
                for k in range(KC):
                    m = pe.matmul(BK[i // 2][0:9, 256 * (i % 2):256 * (i % 2 + 1)].rearrange("p (a n) -> p a n", a=2),
                                  SC[:, k, :], FIRST[i][:, :, 128 * k:128 * (k + 1)], start=k == 0, stop=k == KC - 1,
                                  skip_group_check=True)
                m.then_inc(s_fprod, 1)
            pe.wait_ge(s_cst, 16 * N_CST)
            for b in range(4):
                pe.wait_ge(s_fev, b + 1)
                for i in range(4):
                    c = 9 * (4 * b + i)
                    m = pe.transpose(BK[7][:, c:c + 9], EV[b][:, 128 * i:128 * (i + 1)], IDN[0:9, 0:9])
            m.then_inc(s_ftr, 1)
            pe.wait_ge(s_cst2, 16 * N_CST2)
            pe.wait_ge(s_ones, 1)

            def s5_param(j):
                pe.wait_ge(s_w, j + 1)
                for pl in range(2):
                    for q in range(4):
                        m = pe.transpose(BK[6 + pl][:, 128 * q:128 * (q + 1)],
                                         W2[:, pl, q].rearrange("p s c -> p (s c)"), IDN[:, :])
                    m.then_inc(s_wt, 1)
                pe.wait_ge(s_bd, j + 1)
                pe.wait_ge(s_wtev, 2 * j + 1)
                for q in range(4):
                    for pl in range(2):
                        m = pe.matmul(BK[6][32 * q:32 * (q + 1), 0:128], BD[:, pl, q].rearrange("p a c -> p (a c)"),
                                      PKA[:, PK_CA + 576 * pl + 144 * q:PK_CA + 576 * pl + 144 * q + 128],
                                      start=pl == 0, stop=pl == 1)
                m.then_inc(s_k0, 1)
                pe.wait_ge(s_wtev, 2 * j + 2)
                for pl in range(2):
                    m = pe.transpose(BK[7][:, 128 * pl:128 * (pl + 1)], BD[:, pl].rearrange("p a b c -> p (a b c)"), IDN[:, :])
                m.then_inc(s_bdt, 1)

            pe.wait_ge(s_adaev, 1)
            pe.wait_ge(s_xfree, KC)
            for n in range(KC):
                up_unit(n, n % 4, n, wait_bank=n >= 2, ada=n // 2 + 1)
                if n:
                    pe.wait_ge(s_bdtev, n)
                    pe.wait_ge(s_kr, n)
                s5_param(n)

            def s5_inputs(j, first=False, second=False):
                pe.wait_ge(s_uf, j + 1)
                if not first and not second:
                    pe.wait_ge(s_hl, j - 1)
                for h in range(2):
                    for q in range(4):
                        m = pe.transpose(BK[4 + h][:, 128 * q:128 * (q + 1)], UF[:, 4 * h + q, :], IDN[:, :])
                    m.then_inc(s_tok, 1)
                pe.wait_ge(s_tokev, 2 * j + 2)
                for h in range(2):
                    for q in range(4):
                        m = pe.transpose(BK[4 + h][:, 128 * q:128 * (q + 1)],
                                         UTOK[:, 4 * h + q].rearrange("p s c -> p (s c)"), IDN[:, :])
                    m.then_inc(s_ut, 1)
                pe.wait_ge(s_wtl, 32 * (j + 1))
                pe.wait_ge(s_utev, 2 * j + 2)
                if not first:
                    pe.wait_ge(s_rot, j)
                for q in range(4):
                    for g2 in range(2):
                        for pl in range(2):
                            at = PK_WT + 512 * pl + 128 * q + 64 * g2
                            m = pe.matmul(BK[pl][64 * g2:64 * (g2 + 1), 128 * q:128 * (q + 1)], PKB[:, at:at + 64],
                                          UT[:, 2 * q + g2, :], start=q == 0, stop=True, skip_group_check=True)
                m.then_inc(s_e, 1)

            def s5_toeplitz(j):
                pe.wait_ge(s_tl, 128 * (j + 1))
                for g2 in range(2):
                    for q in range(4):
                        m = pe.matmul(BK[2 + g2][:, 128 * q:128 * (q + 1)], UT[:, 2 * q + g2, :], TT[:, 2 * q + g2, :],
                                      start=q == 0, stop=False, skip_group_check=True)
                m.then_inc(s_tu, 1)
                pe.wait_ge(s_um, j + 1)
                for pl in range(2):
                    m = pe.matmul(BK[6][:, 32 * pl:32 * (pl + 1)], PKB[:, PK_BD + 128 * pl:PK_BD + 128 * (pl + 1)],
                                  UM[:, :, :].rearrange("p a b -> p (a b)"), start=True, stop=True)
                m.then_inc(s_bu, 1)

            def s5_outputs(j):
                pe.wait_ge(s_cal, 32 * (j + 1))
                pe.wait_ge(s_g, j + 1)
                for pl in range(2):
                    m = pe.matmul(BK[7][:, 128:160], PKB[:, PK_CD + 128 * pl:PK_CD + 128 * (pl + 1)],
                                  SSM[:, pl, bass.ds(4 * j, 4), :].rearrange("p a b -> p (a b)"), start=pl == 0, stop=pl == 1)
                for g2 in range(2):
                    rows = slice(64 * g2, 64 * (g2 + 1))
                    for q in range(4):
                        for pl in range(2):
                            at = PK_CA + 576 * pl + 144 * q + 16
                            m = pe.matmul(BK[2 + g2][:, 128 * q:128 * (q + 1)], GS[rows, pl, q, 0:NCH],
                                          PKB[rows, at:at + 128], start=False, stop=True, skip_group_check=True)
                m.then_inc(s_y, 1)
                pe.wait_ge(s_yt, 2 * (j + 1))
                for h in range(2):
                    for q in range(4):
                        m = pe.transpose(BK[4 + h][:, 128 * q:128 * (q + 1)], YT[:, 4 * h + q, :], IDN[:, :])
                    m.then_inc(s_yb, 1)

            pe.wait_ge(s_kr, KC)
            pe.wait_ge(s_bdtev, KC)
            pe.wait_ge(s_ev, 3 * U_S5)
            s5_inputs(0, first=True)
            s5_toeplitz(0)

            def scan_step(j, first):
                s5_inputs(j + 1, second=first)
                s5_outputs(j)
                s5_toeplitz(j + 1)

            scan_step(0, True)
            with pe.Fori(1, KC - 1) as j:
                scan_step(j, False)
            pe.wait_ge(s_ysd, KC - 1)
            s5_outputs(KC - 1)

            pe.wait_ge(s_hl, KC)
            with pe.Fori(0, 4) as a:
                for q in range(4):
                    n = N_GLU + 4 * a + q
                    up_unit(n, q, UP_GLU + 4 * a + q, ada=(UP_GLU + q) // 2 + 1 + 2 * a)

            def down_third(slot, d, g0, t):
                for o in range(KC):
                    i = KC * t + o
                    pe.wait_ge(s_dev, d + i + 1)
                    out = BK[6 + i % 2][:, 0:TH]
                    for q in range(2):
                        sl = (slot + q) % 4
                        wh, wl = WH[:, sl, 128 * o:128 * (o + 1)], WL[:, sl, 128 * o:128 * (o + 1)]
                        gh, gl = GH[:, g0 + q, TH * t:TH * (t + 1)], GL[:, g0 + q, TH * t:TH * (t + 1)]
                        pe.matmul(out, wh, gh, start=q == 0, stop=False)
                        pe.matmul(out, wh, gl, start=False, stop=False)
                        m = pe.matmul(out, wl, gh, start=False, stop=q == 1)
                    m.then_inc(s_down, 1)

            def down_pair(n, slot, d, chunks_ready, g0):
                pe.wait_ge(s_unit, n + 2)
                pe.wait_ge(s_g2, chunks_ready)
                for t in range(3):
                    down_third(slot, d, g0, t)

            def mean(li, t, dev):
                if dev is None or t == 2:
                    pe.wait_ge(s_xr, li + 1)
                else:
                    pe.wait_ge(s_dev, dev + KC * (t + 1) + 2)
                for k in range(KC):
                    m = pe.matmul(BK[t][:, 0:TH], ONES[:, :], X[:, k, TH * t:TH * (t + 1)], start=k == 0, stop=k == KC - 1)
                m.then_inc(s_mean, 1)

            def variance(li, t):
                pe.wait_ge(s_sq, 3 * li + t + 1)
                for k in range(KC):
                    m = pe.matmul(BK[3 + t][:, 0:TH], ONES[:, :], SQB[t % 2][:, k, :], start=k == 0, stop=k == KC - 1)
                m.then_inc(s_var, 1)

            def layer_norm_sums(li, up_done, pair=None):
                dev = None
                if pair is not None:
                    n, slot, dev, chunks_ready, g0 = pair
                    pe.wait_ge(s_unit, n + 2)
                    pe.wait_ge(s_g2, chunks_ready)
                    down_third(slot, dev, g0, 0)
                    down_third(slot, dev, g0, 1)
                pe.wait_ge(s_ev, 3 * up_done)
                mean(li, 0, dev)
                if pair is not None:
                    down_third(slot, dev, g0, 2)
                mean(li, 1, dev)
                if pair is None:
                    mean(li, 2, dev)
                variance(li, 0)
                if pair is not None:
                    mean(li, 2, dev)
                variance(li, 1)
                variance(li, 2)

            def first_two(n0, u0, h_from):
                pe.wait_ge(s_unit, n0 + 2)
                for t in range(3):
                    pe.wait_ge(s_h, h_from + t)
                    pe.wait_ge(s_hlo, h_from + t)
                    if t == 1 and u0 < NADA:
                        for q in range(2):
                            ada_partial(BK[3 * q + 2], q, u0 // 2 + 1)
                    for q in range(2):
                        slot = (n0 + q) % 4
                        if t == 2 and u0 < NADA:
                            pe.wait_ge(s_apart, u0 + q + 1)
                        o = BK[3 * q + t][:, 0:TH]
                        for k in range(KC):
                            wh = WH[:, slot, 128 * k:128 * (k + 1)]
                            wl = WL[:, slot, 128 * k:128 * (k + 1)]
                            hh, hl = HH[:, k, TH * t:TH * (t + 1)], HL[:, k, TH * t:TH * (t + 1)]
                            pe.matmul(o, wh, hh, start=k == 0, stop=False)
                            pe.matmul(o, wh, hl, start=False, stop=False)
                            m = pe.matmul(o, wl, hh, start=False, stop=k == KC - 1)
                        if t == 2 and u0 < NADA:
                            m = ada_sum(BK[3 * q + 2])
                        m.then_inc(s_up, 1)

            def hidden_phase(n0, u0, d0, c0, up_n, groups, h_from):
                def ada(u, a=0):
                    return u // 2 + 1 + 4 * a if u < NADA else None

                first_two(n0, u0, h_from)
                for q in range(2, up_n):
                    up_unit(n0 + q, (n0 + q) % 4, u0 + q, ada=ada(u0 + q))
                per = up_n + 2
                if up_n == 4:
                    with pe.Fori(0, (groups - 1) // 2) as a:
                        for h in range(2):
                            for q in range(up_n):
                                off = up_n + per * h + q
                                u = u0 + up_n * (h + 1) + q
                                up_unit(n0 + off + 2 * per * a, (n0 + off) % 4, u + 2 * up_n * a, ada=ada(u, a))
                            off = 2 * up_n + per * h
                            down_pair(n0 + off + 2 * per * a, (n0 + off) % 4, d0 + 24 * h + 48 * a,
                                      c0 + 2 * h + 2 + 4 * a, 2 * h)
                else:
                    for i in range(groups - 1):
                        for q in range(up_n):
                            off = up_n + per * i + q
                            u = u0 + up_n * (i + 1) + q
                            up_unit(n0 + off, (n0 + off) % 4, u, ada=ada(u))
                        off = 2 * up_n + per * i
                        down_pair(n0 + off, (n0 + off) % 4, d0 + 24 * i, c0 + 2 * i + 2, 2 * (i % 2))
                last = groups - 1
                off = up_n + per * last
                return n0 + off, (n0 + off) % 4, d0 + 24 * last, c0 + 2 * groups, 2 * (last % 2)

            layer_norm_sums(0, UP_F0)
            last_pair = hidden_phase(N_F0, UP_F0, D_F0, C_F0, 4, FC // 2, 1)
            layer_norm_sums(1, UP_SC, last_pair)
            last_pair = hidden_phase(N_SC, UP_SC, D_SC, C_SC, 6, 4, 4)
            layer_norm_sums(2, UP_F1, last_pair)
            last_pair = hidden_phase(N_F1, UP_F1, D_F1, C_F1, 4, FC // 2, 7)
            layer_norm_sums(3, UP_F1 + 2 * FC, last_pair)

        @block.scalar
        def _(act):
            act.wait_ge(s_c, 16)
            act.activation(SC[:, :, :], SC[:, :, :], ACT.Silu).then_inc(s_silu, 1)
            for b in range(4):
                act.wait_ge(s_fprod, 2 * (b + 1))
                act.activation(EV[b], BK[b][0:9, :], ACT.Copy).then_inc(s_fev, 1)
            act.wait_ge(s_adaev, 1)
            for k in range(KC):
                act.wait_ge(s_xin[k], 16)
                if k >= 2:
                    act.wait_ge(s_xfree, k - 1)
                act.activation(XT[k % 2], XIN[k], ACT.Identity, bias=MOD[:, k, 0:1],
                               scale=LC[:, 0, k:k + 1]).then_inc(s_hx, 1)

            def take_mod(u, bank):
                return act.activation(MOD[:, bass.ds(ADA0 + u, 1), :].rearrange("p a b -> p (a b)"),
                                      bank[:, TH:TH + 9], ACT.Identity, bias=BADA[:, bass.ds(ADA0 + u, 1)])

            def take_partial(u, par):
                act.wait_ge(s_ada, u + 1)
                act.activation(EVA[:, :], BK[3 * par + 2][:, TH:TH + 128], ACT.Copy).then_inc(s_apart, 1)

            def take_u(n, par):
                take_partial(n, par)
                for t in range(3):
                    act.wait_ge(s_up, 3 * n + t + 1)
                    if t == 2:
                        take_mod(n, BK[3 * par + 2])
                    act.activation(UALL[:, n, TH * t:TH * (t + 1)],
                                   BK[3 * par + t][:, 0:TH], ACT.Copy).then_inc(s_ev, 1)

            def take_params(j):
                if j:
                    act.wait_ge(s_pk, 16 * j)
                for pl in range(2):
                    act.wait_ge(s_wt, 2 * j + pl + 1)
                    act.activation(PKA[:, PK_WT + 512 * pl:PK_WT + 512 * (pl + 1)], BK[6 + pl][:, :], ACT.Copy)\
                        .then_inc(s_wtev, 1)
                act.wait_ge(s_bdt, j + 1)
                act.activation(PKA[:, PK_BD:PK_BD + 256], BK[7][:, 0:256], ACT.Copy).then_inc(s_bdtev, 1)

            for n in range(KC):
                take_u(n, n % 2)
                take_params(n)

            def s5_stage(j, first):
                act.activation(UF[:, :, :], UALL[:, bass.ds(j, 1), 0:SEQ].rearrange("p a (n s) -> p (a s) n", s=L),
                               ACT.Copy).then_inc(s_uf, 1)
                for h in range(2):
                    act.wait_ge(s_tok, 2 * j + h + 1)
                    act.activation(UTOK[:, :, 4 * h:4 * h + 4, :].rearrange("p g s c -> p s g c"),
                                   BK[4 + h][:, :].rearrange("p (s g c) -> p s g c", s=4, g=8), ACT.Copy).then_inc(s_tokev, 1)
                for h in range(2):
                    act.wait_ge(s_ut, 2 * j + h + 1)
                    if not first:
                        act.wait_ge(s_tu, j)
                    act.activation(UT[:, 4 * h:4 * h + 4, :].rearrange("p g n -> p (g n)"), BK[4 + h][:, :], ACT.Copy)\
                        .then_inc(s_utev, 1)

            def s5_take(j):
                act.wait_ge(s_y, j + 1)
                yv = YT.rearrange("p s (q g c) -> p g q s c", q=4, g=2)
                for g2 in range(2):
                    act.activation(yv[:, g2], BK[2 + g2][:, :].rearrange("p (q s c) -> p q s c", q=4, s=L),
                                   ACT.Gelu_apprx_tanh).then_inc(s_yt, 1)
                hv = HH[:, bass.ds(j, 1), 0:SEQ].rearrange("p a (n s) -> p (a s) n", s=L)
                act.wait_ge(s_yb, 2 * j + 2)
                act.wait_ge(s_ysd, j + 1)
                act.activation(SQ_[:, 6, 8:16], SQ_[:, 6, 0:8], ACT.Gelu_apprx_tanh).then_inc(s_ysg, 1)
                for h in range(2):
                    act.activation(hv[:, 4 * h:4 * h + 4, :], BK[4 + h][:, :].rearrange("p (s n) -> p s n", s=4), ACT.Copy)\
                        .then_inc(s_hhy, 1)

            act.wait_ge(s_ones, 3)
            s5_stage(0, True)
            with act.Fori(0, KC - 1) as j:
                s5_stage(j + 1, False)
                s5_take(j)
            s5_take(KC - 1)

            act.wait_ge(s_xl, 16)

            def glu_rows(n, first):
                for vg in range(2):
                    take_partial(UP_GLU + 2 * n + vg, vg)
                    if vg == 0 and not first:
                        act.wait_ge(s_row, n)
                    for t in range(3):
                        act.wait_ge(s_up, 3 * UP_GLU + 6 * n + 3 * vg + t + 1)
                        m = act.activation((T0, T1)[vg][:, TH * t:TH * (t + 1)], BK[3 * vg + t][:, 0:TH],
                                           (ACT.Copy, ACT.Sigmoid)[vg])
                        if t == 2:
                            m = take_mod(UP_GLU + 2 * n + vg, BK[3 * vg + 2])
                        m.then_inc(s_ev, 1)

            glu_rows(0, True)
            with act.Fori(1, KC) as n:
                glu_rows(n, False)

            def layer_norm(li, last):
                def squares(t):
                    act.wait_ge(s_cent, 3 * li + t + 1)
                    if t == 2:
                        act.wait_ge(s_var, 3 * li + 1)
                    act.activation(SQB[t % 2], X[:, :, TH * t:TH * (t + 1)], ACT.Square).then_inc(s_sq, 1)

                def deviation(t):
                    if t == 2:
                        act.wait_ge(s_xn, 3 * li + 1)
                    act.wait_ge(s_var, 3 * li + t + 1)
                    act.activation(LT[:, t % 2, :], BK[3 + t][:, 0:TH], ACT.Sqrt, bias=EPST[:, :]).then_inc(s_sd, 1)

                def modulate(t):
                    act.wait_ge(s_xn, 3 * li + t + 1)
                    if t == 2 and not last:
                        act.wait_ge(s_h, 3 * li + 1)
                        act.wait_ge(s_hlo, 3 * li + 1)
                    for k in range(KC):
                        xk = X[:, k, TH * t:TH * (t + 1)]
                        if last:
                            act.activation(xk, xk, ACT.Identity, bias=LC[:, 3, k:k + 1], scale=LC[:, 2, k:k + 1]).then_inc(s_y2, 1)
                        else:
                            m = act.activation(HB[t % 2][:, k, :], xk, ACT.Identity, bias=LC[:, 1, k:k + 1], scale=LC[:, 0, k:k + 1])
                            if k % 4 == 3:
                                m.then_inc(s_hh, 1)

                squares(0)
                squares(1)
                if not li:
                    squares(2)
                deviation(0)
                deviation(1)
                modulate(0)
                if li:
                    squares(2)
                deviation(2)
                modulate(1)
                modulate(2)

            def ffn_rows(c, u, rows_done, first, mods):
                if mods and first:
                    take_partial(u, 0)
                act.wait_ge(s_g2, rows_done)
                for vg in range(2):
                    if mods and vg == 1:
                        take_partial(u + 1, 1)
                    Tr, Ur = (T0, U0) if vg == 0 else (T1, U1)
                    row = 2 * c + vg
                    cwr = CWF[:, :, :, :].rearrange("p a b c -> p (a b) c")
                    for t in range(3):
                        act.wait_ge(s_up, 3 * u + 2 * t + vg + 1 if first else 3 * (u + vg) + t + 1)
                        b = BK[3 * vg + t]
                        act.activation(Ur[:, 2 + TH * t:2 + TH * (t + 1)], b[:, 0:TH], ACT.Copy)
                        if t == 2:
                            act.activation(FB[:, bass.ds(row, 1), :].rearrange("p a b -> p (a b)"), b[:, TH - 10:TH], ACT.Copy)
                            if mods:
                                take_mod(u + vg, b)
                        act.activation(Tr[:, TH * t:TH * (t + 1)], b[:, 0:TH], ACT.Identity,
                                       bias=cwr[:, bass.ds(row, 1), 3:4].rearrange("p a b -> p (a b)"),
                                       scale=cwr[:, bass.ds(row, 1), 2:3].rearrange("p a b -> p (a b)")).then_inc(s_ev, 1)

            def ffn_gelu(c_all, slot, c_gelu, next_u):
                act.wait_ge(s_conv, c_gelu)
                act.activation(T1, T1, ACT.Gelu_apprx_tanh).then_inc(s_gelu, 1)
                if next_u is not None:
                    take_partial(next_u, 0)
                act.wait_ge(s_prod, c_all)
                act.activation(GH[:, slot, :], T0, ACT.Copy).then_inc(s_ghi, 1)

            def ffn(u0, c0, gel0):
                def one(slot, c, first=False, last=False):
                    ffn_rows(c, u0 + 2 * c, c0 + c, first, u0 < NADA)
                    ffn_gelu(c0 + c + 1, slot, gel0 + c + 1, u0 + 2 * c + 2 if u0 < NADA and not last else None)
                for c in range(2):
                    one(c, c, first=c == 0)
                with act.Fori(0, 4) as a:
                    for h in range(4):
                        one((2 + h) % 4, 4 * a + 2 + h)
                for c in range(FC - 4, FC):
                    one(c % 4, c, last=c == FC - 1)

            def short_conv(u0, c0):
                for c in range(8):
                    for q in range(3):
                        u = u0 + 3 * c + q
                        if u < NADA:
                            take_partial(u, u % 2)
                        if q == 0:
                            act.wait_ge(s_g2, c0 + c)
                        for t in range(3):
                            act.wait_ge(s_up, 3 * u0 + 2 * t + q + 1 if c == 0 and q < 2 else 3 * u + t + 1)
                            dst = (T1[:, TH * t:TH * (t + 1)], U0[:, 2 + TH * t:2 + TH * (t + 1)],
                                   U1[:, 2 + TH * t:2 + TH * (t + 1)])[q]
                            if t == 2 and u < NADA:
                                take_mod(u, BK[3 * (u % 2) + 2])
                            act.activation(dst, BK[3 * (u % 2) + t][:, 0:TH], ACT.Copy).then_inc(s_ev, 1)
                    act.wait_ge(s_prod, c0 + c + 1)
                    act.activation(GH[:, c % 4, :], T0, ACT.Copy).then_inc(s_ghi, 1)

            layer_norm(0, False)
            act.wait_ge(s_late, 32)
            act.wait_ge(s_h, 3)
            ffn(UP_F0, C_F0, 0)
            layer_norm(1, False)
            act.wait_ge(s_h, 6)
            act.dma_start(fb[0], FB[:, :, :]).then_inc(s_fout, 16)
            act.dma_start(fs1[0], STF[:, :, 1, :]).then_inc(s_fout, 16)
            act.wait_ge(s_fout, 32)
            act.dma_start(CWF[:, :, :, :], cwf[1]).then_inc(s_late, 16)
            act.dma_start(STF[:, :, :, :], stf[1]).then_inc(s_late, 16)
            short_conv(UP_SC, C_SC)
            layer_norm(2, False)
            act.wait_ge(s_late, 64)
            act.wait_ge(s_h, 9)
            ffn(UP_F1, C_F1, FC)
            layer_norm(3, True)

        @block.vector
        def _(dve):
            ts, tt, stt = dve.tensor_scalar, dve.tensor_tensor, dve.scalar_tensor_tensor
            fence = dve.drain
            M, A, S_ = ALU.mult, ALU.add, ALU.subtract

            def q(i):
                return Q[:, i, :]

            MAGIC = 12582912.0

            def rounded(out, x, scale, add=0.0):
                ts(out, x, scale, add, M, A)
                fence()
                ts(out, out, MAGIC, None, A)
                fence()
                ts(out, out, MAGIC, None, S_)
                fence()

            def exact_exp(out, x, n, r, p):
                rounded(n, x, 1.4426950408889634)
                ts(n, n, -126.0, 127.0, ALU.max, ALU.min)
                fence()
                stt(r, n, -0.693359375, x, M, A)
                fence()
                stt(r, n, 2.12194440e-4, r, M, A)
                fence()
                ts(p, r, 1.0 / 40320.0, None, M)
                fence()
                for c in (5040.0, 720.0, 120.0, 24.0, 6.0, 2.0, 1.0):
                    stt(p, p, 1.0 / c, r, A, M)
                    fence()
                ts(p, p, 1.0, None, A)
                ts(n, n, 127.0, None, A)
                fence()
                dve.tensor_copy(QI[:, :], n)
                fence()
                ts(QI[:, :], QI[:, :], 23, None, ALU.logical_shift_left)
                fence()
                tt(out, p, QI[:, :].bitcast(F32), M)
                fence()

            def cmul(o, a, b, t, conj=False):
                tt(t[0], a[0], b[0], M)
                tt(t[1], a[1], b[1], M)
                tt(t[2], a[0], b[1], M)
                tt(t[3], a[1], b[0], M)
                fence()
                tt(o[0], t[0], t[1], S_)
                tt(o[1], t[2], t[3], A)
                fence()

            dve.memset(SCP[:, :, 9:32], 0.0)
            dve.wait_ge(s_silu, 1)
            dve.tensor_copy(SCP[:, :, 0:9], SC[:, :, :])
            dve.wait_ge(s_cst, 16 * N_CST)
            LR, LI, LD = LAM[:, 0, :], LAM[:, 1, :], LAM[:, 2, :]
            exact_exp(q(0), LD, q(1), q(2), q(3))
            tt(q(4), LR, q(0), M)
            tt(q(5), LI, q(0), M)
            fence()
            exact_exp(q(6), q(4), q(1), q(2), q(3))
            rounded(q(7), q(5), 2.0 / math.pi)
            stt(q(8), q(7), -1.5703125, q(5), M, A)
            fence()
            stt(q(8), q(7), -4.837512969970703125e-4, q(8), M, A)
            fence()
            stt(q(8), q(7), -7.54978995489188216e-8, q(8), M, A)
            fence()
            tt(q(9), q(8), q(8), M)
            rounded(q(10), q(7), 0.25, -0.375)
            stt(q(7), q(10), -4.0, q(7), M, A)
            ts(q(11), q(9), 1.0 / 362880.0, None, M)
            ts(q(12), q(9), -1.0 / 3628800.0, None, M)
            fence()
            for cs_, cc_ in ((-1.0 / 5040.0, 1.0 / 40320.0), (1.0 / 120.0, -1.0 / 720.0), (-1.0 / 6.0, 1.0 / 24.0)):
                stt(q(11), q(11), cs_, q(9), A, M)
                stt(q(12), q(12), cc_, q(9), A, M)
                fence()
            stt(q(11), q(11), 1.0, q(8), A, M)
            stt(q(12), q(12), -0.5, q(9), A, M)
            fence()
            ts(q(12), q(12), 1.0, None, A)
            for i in range(4):
                ts(q(13 + i), q(7), float(i), None, ALU.is_equal)
            fence()
            tt(q(13), q(13), q(15), S_)
            tt(q(14), q(14), q(16), S_)
            fence()
            tmp4 = [q(i) for i in range(20, 24)]
            cmul((q(17), q(18)), (q(12), q(11)), (q(13), q(14)), tmp4)
            dve.memset(AP_[:, 0, :, 0:1], 1.0)
            dve.memset(AP_[:, 1, :, 0:1], 0.0)
            ap = lambda pl, k: AP_[:, pl, :, k]
            tt(ap(0, 1), q(17), q(6), M)
            tt(ap(1, 1), q(18), q(6), M)
            fence()
            for k in range(2, KPH):
                cmul((ap(0, k), ap(1, k)), (ap(0, k - 1), ap(1, k - 1)), (ap(0, 1), ap(1, 1)), tmp4)
            for k in range(L):
                dve.tensor_copy(AR[:, :, :, L - 1 - k], AP_[:, :, :, k])
            cur = (q(17), q(18))
            for i in range(3):
                dst = (UP7[:, 0, 0, :], UP7[:, 1, 0, :]) if i == 2 else (q(17), q(18))
                cmul(dst, cur, cur, tmp4)
                tt(RHO[:, :] if i == 2 else q(6), q(6), q(6), M)
                fence()
                cur = dst
            for lv in range(1, 7):
                half = (UP7[:, 0, lv - 1, :], UP7[:, 1, lv - 1, :])
                cmul((UP7[:, 0, lv, :], UP7[:, 1, lv, :]), half, half, tmp4)
            dve.wait_ge(s_ftr, 1)
            tt(MOD[:, 0:16, :], BK[7][:, 0:144].rearrange("p (a b) -> p a b", a=16), bc(BADA[:, 0:16].unsqueeze(2), [128, 16, 9]), A)
            fence()
            ts(LC[:, 0, :], MOD[:, 8:16, 0], 1.0, None, A).then_inc(s_adaev, 1)
            dve.wait_ge(s_cst2, 16 * N_CST2)
            stt(HS[:, :, :], MOD[:, 8:16, 1:9], 1.0, XS[:, :, :], A, M)
            fence()
            tt(HS[:, :, :], HS[:, :, :], MOD[:, 0:8, 1:9], A)
            fence()
            dve.tensor_copy(HH[:, :, SEQ:NT], HS[:, :, :])
            fence()
            tt(HL[:, :, SEQ:NT], HS[:, :, :], HH[:, :, SEQ:NT].bitcast(F32), S_)
            for k in range(KC):
                dve.wait_ge(s_hx, k + 1)
                dve.tensor_copy(HH[:, k, 0:SEQ], XT[k % 2])
                fence()
                tt(HL[:, k, 0:SEQ], XT[k % 2], HH[:, k, 0:SEQ].bitcast(F32), S_).then_inc(s_xfree, 1)

            ts(q(0), ap(0, 1), -1.0, None, A)
            tt(q(1), LR, LR, M)
            tt(q(2), LI, LI, M)
            fence()
            tt(q(1), q(1), q(2), A)
            tt(q(7), q(0), LR, M)
            tt(q(3), ap(1, 1), LI, M)
            tt(q(8), ap(1, 1), LR, M)
            tt(q(5), q(0), LI, M)
            fence()
            dve.reciprocal(q(1), q(1))
            tt(q(2), q(7), q(3), A)
            tt(q(4), q(8), q(5), S_)
            fence()
            tt(q(2), q(2), q(1), M)
            tt(q(4), q(4), q(1), M)
            fence()
            fr, fi = (bc(q(i).unsqueeze(2), [128, NP_, GC]) for i in (2, 4))
            t512 = [TP[:, i, 0:512].rearrange("p (a b) -> p a b", a=NP_) for i in range(2)]
            tt(t512[0], BR[:, 0], fr, M)
            tt(t512[1], BR[:, 1], fi, M)
            fence()
            tt(BB[:, 0], t512[0], t512[1], S_)
            fence()
            tt(t512[0], BR[:, 1], fr, M)
            tt(t512[1], BR[:, 0], fi, M)
            fence()
            tt(BB[:, 1], t512[0], t512[1], A)
            dve.memset(BD[:, :, :, :, :], 0.0)
            dve.memset(PKA[:, PK_CD:PK_CD + 256], 0.0).then_inc(s_pw, 1)

            def s5_params(j, first):
                prs = bass.ds(4 * j, 4)
                av = lambda pl: bc(AR[:, pl, prs, :].unsqueeze(3), [128, 4, L, GC])
                bv = lambda pl: bc(BB[:, pl, prs, :].unsqueeze(2), [128, 4, L, GC])
                t = [TP[:, i, 0:512].rearrange("p (a b c) -> p a b c", a=4, b=L) for i in range(2)]
                fence()
                if not first:
                    dve.wait_ge(s_wt, 2 * j)
                tt(t[0], av(0), bv(0), M)
                tt(t[1], av(1), bv(1), M)
                fence()
                tt(W2[:, 0], t[0], t[1], S_)
                fence()
                tt(t[0], av(0), bv(1), M)
                tt(t[1], av(1), bv(0), M)
                fence()
                tt(W2[:, 1], t[0], t[1], A).then_inc(s_w, 1)
                av9 = lambda pl: bc(AP_[:, pl, prs, :].unsqueeze(3), [128, 4, KPH, GC])
                cv9 = lambda pl: bc(CR[:, pl, prs, :].unsqueeze(2), [128, 4, KPH, GC])
                t = [TP[:, i, :].rearrange("p (a b c) -> p a b c", a=4, b=KPH) for i in range(2)]
                CA = [PKA[:, PK_CA + 576 * pl:PK_CA + 576 * (pl + 1)].rearrange("p (a b c) -> p a b c", a=4, b=KPH)
                      for pl in range(2)]
                fence()
                if not first:
                    dve.wait_ge(s_pk, 16 * j)
                    dve.wait_ge(s_k0, j)
                    dve.wait_ge(s_bdt, j)
                tt(t[0], av9(0), cv9(0), M)
                tt(t[1], av9(1), cv9(1), M)
                fence()
                tt(CA[0], t[0], t[1], S_)
                fence()
                tt(t[0], av9(0), cv9(1), M)
                tt(t[1], av9(1), cv9(0), M)
                fence()
                tf = [TP[:, i, :] for i in range(2)]
                stt(PKA[:, PK_CA + 576:PK_CA + 1152], tf[0], -1.0, tf[1], M, S_)
                CD = PKA[:, PK_CD:PK_CD + 256].rearrange("p (x a b c) -> p x a b c", x=2, a=4, b=2)
                for g2 in range(2):
                    rows = slice(64 * g2, 64 * (g2 + 1))
                    for pl in range(2):
                        dve.tensor_copy(BD[rows, pl, :, g2, :], BB[rows, pl, prs, :])
                        last = ts(CD[rows, pl, :, g2, :], CR[rows, pl, prs, :], 1.0 - 2 * pl, None, M)
                last.then_inc(s_bd, 1)
                dve.wait_ge(s_k0, j + 1)
                if not first:
                    dve.wait_ge(s_krd, 16 * j)
                dve.tensor_copy(KR[:, GC:128], BK[6][:, GC:128])
                stt(KR[:, 0:GC], E16[:, :], DSK[:, bass.ds(j, 1)], BK[6][:, 0:GC], M, A).then_inc(s_kr, 1)
                R = PKA[:, PK_ROT:PK_ROT + 1024].rearrange("p (a b c) -> p a b c", a=2, b=4)
                ur, ui = (bc(UP7[:, pl, 6, prs].unsqueeze(2), [128, 4, 64]) for pl in range(2))
                t = [TP[:, i // 2, 256 * (i % 2):256 * (i % 2 + 1)].rearrange("p (a b) -> p a b", a=4) for i in range(4)]
                dve.wait_ge(s_rtab, j + 1)
                tt(t[0], R[:, 0, :, 0:64], ur, M)
                tt(t[1], R[:, 1, :, 0:64], ui, M)
                tt(t[2], R[:, 0, :, 0:64], ui, M)
                tt(t[3], R[:, 1, :, 0:64], ur, M)
                fence()
                tt(R[:, 0, :, 64:128], t[0], t[1], S_)
                tt(R[:, 1, :, 64:128], t[2], t[3], A).then_inc(s_rot6, 1)

            s5_params(0, True)
            with dve.Fori(1, KC) as j:
                s5_params(j, False)

            def masked_u(j, first):
                if not first:
                    dve.wait_ge(s_bu, j)
                tt(UM[:, :, :], PM[:, :, :], bc(UALL[:, bass.ds(j, 1), SEQ:NT], [128, 4, NS]), M).then_inc(s_um, 1)

            def s5_states(j, first):
                dve.wait_ge(s_e, j + 1)
                dve.wait_ge(s_rl, 16 * (j + 1))
                RC = PKB[:, PK_ROT:PK_ROT + 512].rearrange("p (a b) -> p a b", a=4)
                RS = PKB[:, PK_ROT + 512:PK_ROT + 1024].rearrange("p (a b) -> p a b", a=4)
                ER, EI = (BK[i][:, :].rearrange("p (a b) -> p a b", a=4) for i in range(2))
                v = [TQ[:, i] for i in range(4)]
                tt(v[0], ER, RC, M)
                tt(v[3], ER, RS, M)
                tt(v[1], EI, RS, M)
                tt(v[2], EI, RC, M).then_inc(s_rot, 1)
                fence()
                tt(v[0], v[0], v[1], A)
                tt(v[2], v[2], v[3], S_)
                fence()
                for p in range(4):
                    for pl in range(2):
                        dve.tensor_tensor_scan(TQ[:, 2 * pl + 1, p, :], bc(RHO[:, bass.ds(4 * j + p, 1)], [128, NCH]),
                                               TQ[:, 2 * pl, p, :], 0.0, M, A)
                fence()

            def s5_states_out(j, first):
                RC = PKB[:, PK_ROT:PK_ROT + 512].rearrange("p (a b) -> p a b", a=4)
                RS = PKB[:, PK_ROT + 512:PK_ROT + 1024].rearrange("p (a b) -> p a b", a=4)
                v = [TQ[:, i] for i in range(4)]
                tt(v[0], v[1], RC, M)
                tt(v[2], v[3], RS, M)
                fence()
                if not first:
                    dve.wait_ge(s_y, j)
                tt(GS[:, 0, :, 1:NCH + 1], v[0], v[2], S_)
                fence()
                tt(v[0], v[1], RS, M)
                tt(v[2], v[3], RC, M)
                fence()
                tt(GS[:, 1, :, 1:NCH + 1], v[0], v[2], A)
                prs = bass.ds(4 * j, 4)
                a1 = [bc(AP_[:, pl, prs, 1:2], [128, 4, NS]) for pl in range(2)]
                h0 = [H0[:, pl, prs, :] for pl in range(2)]
                w = [SQ_[:, i, :].rearrange("p (a b) -> p a b", a=4) for i in range(4)]
                dve.wait_ge(s_bu, j + 1)
                tt(w[0], a1[0], h0[0], M)
                tt(w[1], a1[1], h0[1], M)
                tt(w[2], a1[0], h0[1], M)
                tt(w[3], a1[1], h0[0], M)
                fence()
                dve.tensor_copy(SFIN[:, :, prs], GS[:, :, :, NCH])
                tt(w[0], w[0], w[1], S_)
                tt(w[2], w[2], w[3], A)
                fence()
                tt(SSM[:, 0, prs, :], BK[6][:, 0:32].rearrange("p (a b) -> p a b", a=4), w[0], A)
                tt(SSM[:, 1, prs, :], BK[6][:, 32:64].rearrange("p (a b) -> p a b", a=4), w[2], A).then_inc(s_g, 1)

            def s5_split(j):
                dve.wait_ge(s_y, j + 1)
                w = SQ_[:, 4, :].rearrange("p (a b) -> p a b", a=4)
                tt(w, BK[7][:, 128:160].rearrange("p (a b) -> p a b", a=4), PM[:, :, :], M)
                fence()
                dve.tensor_reduce(SQ_[:, 5, 0:8], w.rearrange("p a b -> p b a"), mybir.AxisListType.X, A)
                fence()
                us = UALL[:, bass.ds(j, 1), SEQ:NT].rearrange("p a b -> p (a b)")
                stt(SQ_[:, 6, 0:8], us, DSK[:, bass.ds(j, 1)], SQ_[:, 5, 0:8], M, A).then_inc(s_ysd, 1)
                lv = HL[:, bass.ds(j, 1), 0:SEQ].rearrange("p a (n s) -> p (a s) n", s=L)
                hv = HH[:, bass.ds(j, 1), 0:SEQ].rearrange("p a (n s) -> p (a s) n", s=L).bitcast(F32)
                for h in range(2):
                    dve.wait_ge(s_hhy, 2 * j + h + 1)
                    tt(lv[:, 4 * h:4 * h + 4, :], BK[4 + h][:, :].rearrange("p (s n) -> p s n", s=4), hv[:, 4 * h:4 * h + 4, :], S_)
                dve.wait_ge(s_ysg, j + 1)
                hs = HH[:, bass.ds(j, 1), SEQ:NT].rearrange("p a b -> p (a b)")
                ls = HL[:, bass.ds(j, 1), SEQ:NT].rearrange("p a b -> p (a b)")
                dve.tensor_copy(hs, SQ_[:, 6, 8:16])
                fence()
                tt(ls, SQ_[:, 6, 8:16], hs.bitcast(F32), S_).then_inc(s_hl, 1)

            dve.wait_ge(s_ones, 3)
            masked_u(0, True)
            s5_states(0, True)
            s5_states_out(0, True)
            masked_u(1, False)

            def scan_step(j, more):
                s5_states(j, False)
                s5_split(j - 1)
                s5_states_out(j, False)
                if more:
                    masked_u(j + 1, False)

            with dve.Fori(1, KC - 1) as j:
                scan_step(j, True)
            scan_step(KC - 1, False)
            s5_split(KC - 1)

            dve.wait_ge(s_xl, 16)
            with dve.Fori(0, KC) as n:
                xn = X[:, bass.ds(n, 1), :].rearrange("p a b -> p (a b)")
                gm = MOD[:, bass.ds(16 + n, 1), :].rearrange("p a b -> p (a b)")
                ts(xn, xn, ALPHA, None, M)
                dve.wait_ge(s_ev, 3 * (UP_GLU + 2) + 6 * n)
                tt(T0, T0, T1, M)
                fence()
                stt(xn[:, 0:SEQ], T0[:, 0:SEQ], gm[:, 0:1], xn[:, 0:SEQ], M, A)
                tt(T1[:, SEQ:NT], T0[:, SEQ:NT], gm[:, 1:9], M)
                fence()
                tt(xn[:, SEQ:NT], xn[:, SEQ:NT], T1[:, SEQ:NT], A).then_inc(s_row, 1)
            dve.memset(FSA[:, 0:4, :], 0.0).then_inc(s_dev, 2)
            dve.memset(FSA[:, 4:8, :], 0.0).then_inc(s_xr, 1)

            def ln_constants(li, last):
                g, b = LNP[:, li, 0, :], LNP[:, li, 1, :]
                al = 1.0 if last else ALPHA
                fence()
                ts(LC[:, 2, :], g, al, None, M)
                ts(LC[:, 3, :], b, al, None, M)
                if not last:
                    sh, sc = (MOD[:, 8 * (3 * li + 3) + 8 * i:8 * (3 * li + 3) + 8 * (i + 1), 0] for i in range(2))
                    stt(LC[:, 0, :], sc, 1.0, g, A, M)
                    stt(LC[:, 1, :], sc, 1.0, b, A, M)
                    fence()
                    tt(LC[:, 1, :], LC[:, 1, :], sh, A)
                fence()

            def take_third(d, gsec, t):
                w = TH if t < 2 else PT2
                for o in range(KC):
                    i = KC * t + o
                    b = BK[6 + i % 2]
                    dve.wait_ge(s_down, d + i + 1)
                    if t == 2:
                        tt(FSA[:, o, :], FSA[:, o, :], b[:, PT2:TH], A)
                    xo = X[:, o, TH * t:TH * t + w]
                    stt(xo, b[:, 0:w], MOD[:, gsec + o, 0:1], xo, M, A).then_inc(s_dev, 1)

            def take_down(d, gsec):
                for t in range(3):
                    take_third(d, gsec, t)

            def end_down(gsec):
                fence()
                tt(FSA[:, :, :], FSA[:, :, :], MOD[:, gsec:gsec + 8, 1:9], M)
                fence()
                tt(X[:, :, SEQ:NT], X[:, :, SEQ:NT], FSA[:, :, :], A)
                fence()
                dve.memset(FSA[:, :, :], 0.0).then_inc(s_xr, 1)

            def layer_norm(li, last, d=None, gsec=None):
                cols = [slice(TH * t, TH * (t + 1)) for t in range(3)]

                def center(t):
                    dve.wait_ge(s_mean, 3 * li + t + 1)
                    tt(X[:, :, cols[t]], X[:, :, cols[t]], bc(BK[t][:, 0:TH].unsqueeze(1), [128, KC, TH]), S_).then_inc(s_cent, 1)

                def scale(t):
                    fence()
                    dve.wait_ge(s_sd, 3 * li + t + 1)
                    dve.reciprocal(LT[:, 2, :], LT[:, t % 2, :])
                    fence()
                    stt(LT[:, 3, :], LT[:, 2, :], -0.5, LT[:, 2, :], M, M)
                    fence()
                    stt(LT[:, 3, :], BK[3 + t][:, 0:TH], EPS, LT[:, 3, :], A, M)
                    fence()
                    stt(LT[:, 2, :], LT[:, 3, :], 1.5, LT[:, 2, :], A, M)
                    fence()
                    tt(X[:, :, cols[t]], X[:, :, cols[t]], bc(LT[:, 2:3, :], [128, KC, TH]), M).then_inc(s_xn, 1)

                def split(t):
                    hb = HB[t % 2]
                    if t == 2:
                        xs = X[:, :, SEQ:NT]
                        gb = [bc(LNP[:, li, i, :].unsqueeze(2), [128, KC, NS]) for i in range(2)]
                        o = 8 * (3 * li + 3)
                        fence()
                        tt(SMP[:, 0], xs, gb[0], M)
                        fence()
                        tt(SMP[:, 0], SMP[:, 0], gb[1], A)
                        fence()
                        stt(SMP[:, 1], MOD[:, o + 8:o + 16, 1:9], 1.0, SMP[:, 0], A, M)
                        fence()
                        dve.wait_ge(s_hh, 2 * (3 * li + t) + 2)
                        tt(hb[:, :, PT2:TH], SMP[:, 1], MOD[:, o:o + 8, 1:9], A)
                        fence()
                    for h in range(2):
                        dve.wait_ge(s_hh, 2 * (3 * li + t) + h + 1)
                        m = dve.tensor_copy(HH[:, 4 * h:4 * h + 4, cols[t]], hb[:, 4 * h:4 * h + 4, :])
                    m.then_inc(s_hhi, 1)
                    fence()
                    if t == 2:
                        dve.memset(U0[:, 0:2], 0.0)
                        dve.memset(U1[:, 0:2], 0.0)
                    tt(HL[:, 0:KD, cols[t]], hb[:, 0:KD], HH[:, 0:KD, cols[t]].bitcast(F32), S_).then_inc(s_h, 1)

                if d is not None:
                    take_third(d, gsec, 0)
                    take_third(d, gsec, 1)
                center(0)
                if d is not None:
                    take_third(d, gsec, 2)
                    end_down(gsec)
                center(1)
                ln_constants(li, last)
                if d is None:
                    center(2)
                scale(0)
                if d is not None:
                    center(2)
                scale(1)
                if not last:
                    split(0)
                scale(2)
                if not last:
                    split(1)
                    split(2)

            def hidden_split(c_all, slot):
                dve.wait_ge(s_ghi, c_all)
                tt(GL[:, slot, :], T0, GH[:, slot, :].bitcast(F32), S_).then_inc(s_g2, 1)

            def ffn_conv(cc, u0):
                cwr = CWF[:, :, :, :].rearrange("p a b c -> p (a b) c")
                for vg in range(2):
                    Tr, Ur = (T0, U0) if vg == 0 else (T1, U1)
                    row = 2 * cc + vg
                    cw = [cwr[:, bass.ds(row, 1), i:i + 1].rearrange("p a b -> p (a b)") for i in range(2)]
                    st = [STF[:, bass.ds(row, 1), i, :].rearrange("p a b -> p (a b)") for i in range(2)]
                    dve.wait_ge(s_ev, 3 * (u0 + 1 + vg) + 6 * cc)
                    stt(Tr[:, 0:SEQ], Ur[:, 1:1 + SEQ], cw[1], Tr[:, 0:SEQ], M, A)
                    stt(Tr[:, SEQ:NT], st[1], cw[1], Tr[:, SEQ:NT], M, A)
                    fence()
                    stt(Tr[:, SEQ:NT], st[0], cw[0], Tr[:, SEQ:NT], M, A)
                    last = stt(Tr[:, 0:SEQ], Ur[:, 0:SEQ], cw[0], Tr[:, 0:SEQ], M, A)
                last.then_inc(s_conv, 1)

            def ffn_product(cc, gel0):
                dve.wait_ge(s_gelu, gel0 + 1 + cc)
                tt(T0, T0, T1, M).then_inc(s_prod, 1)

            def ffn_work(cc, u0, c0, gel0, slot):
                ffn_conv(cc, u0)
                ffn_product(cc, gel0)
                hidden_split(c0 + 1 + cc, slot)

            def ffn(u0, c0, d0, gel0, gsec, xup):
                for c in range(2):
                    ffn_work(c, u0, c0, gel0, c)
                dve.wait_ge(s_xup, xup)

                def two_groups(a, count):
                    for h in range(count):
                        ffn_work(4 * a + 2 + 2 * h, u0, c0, gel0, (2 + 2 * h) % 4)
                        if h == 0:
                            dve.wait_ge(s_ev, 3 * (u0 + 8) + 24 * a)
                        take_down(d0 + 48 * a + 24 * h, gsec)
                        ffn_work(4 * a + 3 + 2 * h, u0, c0, gel0, (3 + 2 * h) % 4)

                with dve.Fori(0, 4) as a:
                    two_groups(a, 2)
                two_groups(4, 1)
                ffn_work(FC - 2, u0, c0, gel0, (FC - 2) % 4)
                d = d0 + 24 * (FC // 2 - 2)
                ffn_conv(FC - 1, u0)
                take_third(d, gsec, 0)
                ffn_product(FC - 1, gel0)
                take_third(d, gsec, 1)
                hidden_split(c0 + FC, (FC - 1) % 4)
                take_third(d, gsec, 2)

            def short_conv(u0, c0, d0, gsec):
                def product(c):
                    dve.wait_ge(s_ev, 3 * (u0 + 3 * c + 3))
                    tt(U0[:, 2:2 + NT], U0[:, 2:2 + NT], U1[:, 2:2 + NT], M)
                    fence()
                    w0, w1, w2 = (CWC[:, c, i:i + 1] for i in range(3))
                    dve.tensor_copy(CB[:, c, :], U0[:, NT + 2 - 10:NT + 2])
                    ts(T0, U0[:, 2:2 + NT], w2, None, M)
                    fence()
                    stt(T0[:, 0:SEQ], U0[:, 1:1 + SEQ], w1, T0[:, 0:SEQ], M, A)
                    stt(T0[:, SEQ:NT], STC[:, c, 1, :], w1, T0[:, SEQ:NT], M, A)
                    fence()
                    stt(T0[:, SEQ:NT], STC[:, c, 0, :], w0, T0[:, SEQ:NT], M, A)
                    stt(T0[:, 0:SEQ], U0[:, 0:SEQ], w0, T0[:, 0:SEQ], M, A)
                    fence()
                    tt(T0, T0, T1, M).then_inc(s_prod, 1)

                def work(c):
                    product(c)
                    hidden_split(c0 + 1 + c, c % 4)

                work(0)
                work(1)
                dve.wait_ge(s_xup, 2)
                for i in range(1, 3):
                    work(2 * i)
                    take_down(d0 + 24 * (i - 1), gsec)
                    work(2 * i + 1)
                work(6)
                product(7)
                take_third(d0 + 48, gsec, 0)
                hidden_split(c0 + 8, 7 % 4)
                take_third(d0 + 48, gsec, 1)
                take_third(d0 + 48, gsec, 2)

            layer_norm(0, False)
            dve.wait_ge(s_late, 32)
            ffn(UP_F0, C_F0, D_F0, 0, 40, 1)
            layer_norm(1, False, D_F0 + 24 * (FC // 2 - 1), 40)
            short_conv(UP_SC, C_SC, D_SC, 64)
            layer_norm(2, False, D_SC + 72, 64)
            dve.wait_ge(s_late, 64)
            ffn(UP_F1, C_F1, D_F1, FC, 88, 3)
            layer_norm(3, True, D_F1 + 24 * (FC // 2 - 1), 88)



def _features(a):
    a = np.moveaxis(a, -1, 0)
    return np.ascontiguousarray(np.moveaxis(a.reshape((-1, 128) + a.shape[1:]), 0, 1))


def _up_units(w):
    return w.reshape(KC, 128, -1, 128).transpose(2, 1, 0, 3).reshape(-1, 128, 1024)


def _down_units(w):
    return w.reshape(-1, 128, 1024)


def _phase(ups, downs, up_n):
    groups = len(downs) // 2
    ups = ups.reshape(groups, up_n, 128, 1024)
    downs = downs.reshape(groups, 2, 128, 1024)
    parts = [ups[0]]
    for i in range(1, groups):
        parts += [ups[i], downs[i - 1]]
    return parts + [downs[-1]]


def _pairs(a):
    a = a.reshape((NP_, 2, P) + a.shape[2:])
    return np.moveaxis(a, 0, 2).reshape((128, NP_) + a.shape[3:])


def kernel(**inputs):
    import concourse.bacc as bacc
    from concourse.bass_utils import run_bass_kernel_spmd

    v = {k: np.asarray(a) for k, a in inputs.items()}
    ffn = []
    for i in range(2):
        up = _up_units(v["ffn_w_up"][i]).reshape(2, FC, 128, 1024).swapaxes(0, 1).reshape(-1, 128, 1024)
        ffn.append(_phase(up, _down_units(v["ffn_w_down"][i]), 4))
    glu = _up_units(v["s5_w_glu"][0]).reshape(2, KC, 128, 1024).swapaxes(0, 1).reshape(-1, 128, 1024)
    scu = _up_units(v["sc_w_in"][0]).reshape(3, KC, 128, 1024).swapaxes(0, 1).reshape(-1, 128, 1024)
    stream = np.concatenate([_up_units(v["s5_w_in"][0]), glu] + ffn[0]
                            + _phase(scu, _down_units(v["sc_w_out"][0]), 6) + ffn[1])
    p = np.arange(128)
    x_all = np.concatenate([v["x_prompt"][0], v["x_sample"][:, 0]])
    c_all = np.concatenate([v["c_prompt"], v["c_sample"]])
    cwf = np.concatenate([v["ffn_conv_w"], v["ffn_conv_b"][:, None]], 1)
    ins = {
        "xT": _features(x_all), "cT": _features(c_all),
        "wada": _up_units(v["w_ada"]), "bada": _features(v["b_ada"]),
        "wstream": stream,
        "lam": np.stack([_pairs(v["s5_lam_re"][0]), _pairs(v["s5_lam_im"][0]),
                         _pairs(np.repeat(v["s5_log_dt"][0][:, None], P, 1))], 1),
        "bT": np.stack([_pairs(v["s5_b_re"][0]), _pairs(v["s5_b_im"][0])]),
        "cS": np.stack([_pairs(v["s5_c_re"][0].swapaxes(1, 2)), _pairs(v["s5_c_im"][0].swapaxes(1, 2))]),
        "dT": _features(v["s5_d"][0]),
        "h0T": np.stack([_pairs(np.moveaxis(v[n][0], 0, 2)) for n in ("state_s5_re", "state_s5_im")], 1),
        "ident": np.eye(128, dtype=np.float32),
        "stack": (p[:, None] % 32 == np.arange(9)).astype(np.float32),
        "eye16": (p[:, None] % GC == np.arange(GC)).astype(np.float32),
        "pmask": np.repeat((p[:, None] // 32 == np.arange(4)).astype(np.float32)[:, :, None], NS, 2),
        "lnp": np.stack([_features(v[n].reshape(4, D)).transpose(0, 2, 1) for n in ("ln_g", "ln_b")], 2),
        "cwf": np.stack([_features(cwf[i]).reshape(128, 2, FC, 4).swapaxes(1, 2) for i in range(2)]),
        "cwc": _features(v["sc_conv_w"][0]),
        "stf": np.stack([_features(v["state_ffn"][i].swapaxes(0, 1)).reshape(128, 2, FC, 2, NS).swapaxes(1, 2)
                         .reshape(128, 2 * FC, 2, NS) for i in range(2)]),
        "stc": _features(v["state_conv"][0].swapaxes(0, 1)),
    }
    outs = {"yT": (128, KC, NT), "sfin": (128, 2, NP_), "ssm": (128, 2, NP_, NS), "fb": (2, 128, 2 * FC, 10),
            "fs1": (2, 128, 2 * FC, NS), "cb": (128, KC, 10), "cs1": (128, KC, NS)}
    nc = bacc.Bacc("TRN2", target_bir_lowering=False, num_devices=1)
    arrays, args = {}, {}
    for name, a in ins.items():
        arrays[f"in_{name}"] = np.ascontiguousarray(a)
        args[name] = nc.dram_tensor(f"in_{name}", a.shape, F32, kind="ExternalInput").ap()
    for name, shape in outs.items():
        args[name] = nc.dram_tensor(f"out_{name}", shape, F32, kind="ExternalOutput").ap()
    trunk_kernel(nc, **args)
    r = run_bass_kernel_spmd(nc, [arrays], core_ids=[0]).results[0]
    o = {name: np.asarray(r[f"out_{name}"]) for name in outs}

    def tokens(a):
        return a.transpose(2, 1, 0).reshape(a.shape[2], -1)

    def groups(a):
        a = a.reshape((2, P) + a.shape[1:])
        return np.moveaxis(a, 2, 0).reshape((G, P) + a.shape[3:])

    def rows(a):
        a = a.reshape(128, FC, 2, -1)
        return a.transpose(3, 2, 1, 0).reshape(a.shape[3], 2 * DFF)

    y = tokens(o["yT"])
    new_f = [rows(o["fb"][i]) for i in range(2)]
    old_f = [rows(o["fs1"][i]) for i in range(2)]
    new_c, old_c = tokens(o["cb"]), tokens(o["cs1"])
    sre, sim = (groups(o["ssm"][:, i]) for i in range(2))
    got = (
        y[None, :SEQ], y[SEQ:, None],
        groups(o["sfin"][:, 0])[None, None], groups(o["sfin"][:, 1])[None, None],
        np.moveaxis(sre, 2, 0)[None], np.moveaxis(sim, 2, 0)[None],
        new_c[None, None, :2], np.stack([old_c, new_c[2:]], 1)[None],
        np.stack([f[None, :2] for f in new_f]),
        np.stack([np.stack([o_, f[2:]], 1) for o_, f in zip(old_f, new_f)]),
    )
    return tuple(np.ascontiguousarray(a) for a in got)
```
